# Optimizing a Trainium2 kernel written in Bass

```python
import jax
import jax.numpy as jnp
from jax import lax
import numpy as np

D_MODEL = 1024
BATCH = 1
SEQ = 128
DEPTH = 2
DEC_BATCH = 1
DEC_SEQ = 512
PAST_LEN = 128

GRID_W = 64
N_MIXERS = 2
N_NA_LAYERS = (DEPTH + 1) // 2
N_MLA_LAYERS = DEPTH // 2
NA_HEADS = 16
NA_HEAD_DIM = D_MODEL // NA_HEADS
NA_KH = 8
NA_KW = 16
NA_QB = NA_KW
NA_KB = 2 * NA_KW
MLA_HEADS = 16
MLA_Q_RANK = 384
MLA_KV_RANK = 256
MLA_NOPE_DIM = 64
MLA_ROPE_DIM = 32
MLA_V_DIM = 64
MLA_QK_DIM = MLA_NOPE_DIM + MLA_ROPE_DIM
ROPE_THETA = 10000.0
Q_BLOCK = 128
N_GROUPS = 4
EXPERTS_PER_GROUP = 4
N_EXPERTS = N_GROUPS * EXPERTS_PER_GROUP
TOP_K_IN_GROUP = 2
D_FF_EXPERT = 256
N_MOD = 6
EPS = 1e-6
NEG_INF = -1e30

kernel_name = "hybrid_natten_mla_hmoe_diffusion_step"

def rms_norm(x, g):
    xf = x.astype(jnp.float32)
    y = xf * lax.rsqrt(jnp.mean(xf * xf, axis=-1, keepdims=True) + EPS)
    return (y * g.astype(jnp.float32)).astype(x.dtype)

def ada_params(cond, w, b):
    m = (jax.nn.silu(cond) @ w + b)[..., None, :]
    return jnp.split(m, N_MOD, axis=-1)

def modulate(h, shift, scale):
    return h * (1 + scale) + shift

def axial_rope_tables(n_tokens):
    n_freq = MLA_ROPE_DIM // 4
    inv = 1.0 / (ROPE_THETA ** (jnp.arange(n_freq, dtype=jnp.float32) / n_freq))
    t = jnp.arange(n_tokens)
    row = (t // GRID_W).astype(jnp.float32)
    col = (t % GRID_W).astype(jnp.float32)
    ang = jnp.concatenate([row[:, None] * inv, col[:, None] * inv], axis=-1)
    return jnp.cos(ang), jnp.sin(ang)

def apply_rope(x, cos, sin):
    x1, x2 = jnp.split(x, 2, axis=-1)
    return jnp.concatenate([x1 * cos - x2 * sin, x2 * cos + x1 * sin], axis=-1).astype(x.dtype)

def block_attention(q, k, v, scale):
    b, tq, h, dk = q.shape
    nb = tq // Q_BLOCK
    qb = jnp.moveaxis(q.reshape(b, nb, Q_BLOCK, h, dk), 1, 0)

    def one(qi):
        s = jnp.einsum('bqhd,bkhd->bhqk', qi, k, preferred_element_type=jnp.float32) * scale
        p = jax.nn.softmax(s, axis=-1).astype(v.dtype)
        return jnp.einsum('bhqk,bkhd->bqhd', p, v)

    o = lax.map(one, qb)
    return jnp.moveaxis(o, 0, 1).reshape(b, tq, h, v.shape[-1])

def na_window_indices(rows):
    kh = min(NA_KH, rows)
    n_cb = GRID_W // NA_QB
    r = np.arange(rows)
    row_idx = np.clip(r - kh // 2, 0, rows - kh)[:, None] + np.arange(kh)[None, :]
    q_col = np.arange(n_cb)[:, None] * NA_QB + np.arange(NA_QB)[None, :]
    cb_start = np.clip(np.arange(n_cb) * NA_QB - NA_KW // 2, 0, GRID_W - NA_KB)
    col_idx = cb_start[:, None] + np.arange(NA_KB)[None, :]
    col_start = np.clip(q_col - NA_KW // 2, 0, GRID_W - NA_KW)
    kc = col_idx[:, None, :]
    col_valid = (kc >= col_start[:, :, None]) & (kc < col_start[:, :, None] + NA_KW)
    dy_idx = row_idx - r[:, None] + (NA_KH - 1)
    dx_idx = np.clip(kc - q_col[:, :, None] + (NA_KW - 1), 0, 2 * NA_KW - 2)
    return row_idx, col_idx, col_valid, dy_idx, dx_idx

def na_context(h, w_qkv, w_o):
    b, t, _ = h.shape
    q, k, v = [a.reshape(b, t, NA_HEADS, NA_HEAD_DIM) for a in jnp.split(h @ w_qkv, 3, axis=-1)]
    o = block_attention(q, k, v, NA_HEAD_DIM ** -0.5)
    return o.reshape(b, t, D_MODEL) @ w_o, k, v

def na_latent(h, k_ctx, v_ctx, w_qkv, rpb, w_o, idx):
    row_idx, col_idx, col_valid, dy_idx, dx_idx = idx
    b, t, _ = h.shape
    rows = t // GRID_W
    n_cb = GRID_W // NA_QB
    scale = NA_HEAD_DIM ** -0.5
    q, k, v = jnp.split(h @ w_qkv, 3, axis=-1)
    q = q.reshape(b, rows, n_cb, NA_QB, NA_HEADS, NA_HEAD_DIM)
    k = k.reshape(b, rows, GRID_W, NA_HEADS, NA_HEAD_DIM)
    v = v.reshape(b, rows, GRID_W, NA_HEADS, NA_HEAD_DIM)
    ri = row_idx[:, None, :, None]
    ci = col_idx[None, :, None, :]
    k_win = k[:, ri, ci]
    v_win = v[:, ri, ci]
    s_win = jnp.einsum('brnqhd,brnykhd->bhrnqyk', q, k_win, preferred_element_type=jnp.float32) * scale
    bias = rpb[:, dy_idx[:, None, None, :, None], dx_idx[None, :, :, None, :]]
    s_win = jnp.where(col_valid[:, :, None, :], s_win + bias.astype(jnp.float32), NEG_INF)
    s_ctx = jnp.einsum('brnqhd,bchd->bhrnqc', q, k_ctx, preferred_element_type=jnp.float32) * scale
    n_win = row_idx.shape[1] * NA_KB
    s = jnp.concatenate([s_win.reshape(*s_win.shape[:5], n_win), s_ctx], axis=-1)
    p = jax.nn.softmax(s, axis=-1).astype(v.dtype)
    p_win = p[..., :n_win].reshape(s_win.shape)
    p_ctx = p[..., n_win:]
    o = (jnp.einsum('bhrnqyk,brnykhd->brnqhd', p_win, v_win)
         + jnp.einsum('bhrnqc,bchd->brnqhd', p_ctx, v_ctx))
    return o.reshape(b, t, D_MODEL) @ w_o

def mla_project(h, w_in, q_norm_g, kv_norm_g, w_uq):
    b, t, _ = h.shape
    c_q, c_kv, k_rope = jnp.split(h @ w_in, [MLA_Q_RANK, MLA_Q_RANK + MLA_KV_RANK], axis=-1)
    q = (rms_norm(c_q, q_norm_g) @ w_uq).reshape(b, t, MLA_HEADS, MLA_QK_DIM)
    return q, rms_norm(c_kv, kv_norm_g), k_rope

def mla_keys_values(c_kv, k_rope, w_uk, w_uv):
    b, t, _ = c_kv.shape
    k_nope = (c_kv @ w_uk).reshape(b, t, MLA_HEADS, MLA_NOPE_DIM)
    k_r = jnp.broadcast_to(k_rope[:, :, None, :], (b, t, MLA_HEADS, MLA_ROPE_DIM))
    v = (c_kv @ w_uv).reshape(b, t, MLA_HEADS, MLA_V_DIM)
    return jnp.concatenate([k_nope, k_r], axis=-1), v

def mla_context(h, w_in, q_norm_g, kv_norm_g, w_uq, w_uk, w_uv, w_o):
    b, t, _ = h.shape
    q, c_kv, k_rope = mla_project(h, w_in, q_norm_g, kv_norm_g, w_uq)
    k, v = mla_keys_values(c_kv, k_rope, w_uk, w_uv)
    o = block_attention(q, k, v, MLA_QK_DIM ** -0.5)
    return o.reshape(b, t, MLA_HEADS * MLA_V_DIM) @ w_o, c_kv, k_rope

def mla_latent(h, ckv_ctx, kr_ctx, cos, sin, w_in, q_norm_g, kv_norm_g, w_uq, w_uk, w_uv, w_o):
    b, t, _ = h.shape
    q, c_kv, k_rope = mla_project(h, w_in, q_norm_g, kv_norm_g, w_uq)
    q = jnp.concatenate([q[..., :MLA_NOPE_DIM],
                         apply_rope(q[..., MLA_NOPE_DIM:], cos[:, None, :], sin[:, None, :])], axis=-1)
    k_lat, v_lat = mla_keys_values(c_kv, apply_rope(k_rope, cos, sin), w_uk, w_uv)
    k_ctx, v_ctx = mla_keys_values(ckv_ctx, kr_ctx, w_uk, w_uv)
    k = jnp.concatenate([k_lat, k_ctx], axis=1)
    v = jnp.concatenate([v_lat, v_ctx], axis=1)
    o = block_attention(q, k, v, MLA_QK_DIM ** -0.5)
    return o.reshape(b, t, MLA_HEADS * MLA_V_DIM) @ w_o

def hier_moe(h, w_group, b_group, w_expert, b_expert, w_gate, w_up, w_down):
    shp = h.shape
    x = h.reshape(-1, D_MODEL)
    n = x.shape[0]
    g_logits = jnp.dot(x, w_group, preferred_element_type=jnp.float32) + b_group.astype(jnp.float32)
    g_sel = jnp.argmax(g_logits, axis=-1)
    p_group = jnp.take_along_axis(jax.nn.softmax(g_logits, axis=-1), g_sel[:, None], axis=-1)
    e_logits = (jnp.dot(x, w_expert, preferred_element_type=jnp.float32)
                + b_expert.astype(jnp.float32)).reshape(n, N_GROUPS, EXPERTS_PER_GROUP)
    e_in = jnp.take_along_axis(e_logits, g_sel[:, None, None], axis=1)[:, 0]
    top_val, top_idx = lax.top_k(e_in, TOP_K_IN_GROUP)
    w_top = jax.nn.softmax(top_val, axis=-1) * p_group
    ids = g_sel[:, None] * EXPERTS_PER_GROUP + top_idx
    gates = jnp.einsum('nk,nke->ne', w_top, jax.nn.one_hot(ids, N_EXPERTS, dtype=jnp.float32)).astype(x.dtype)
    hid = jax.nn.silu(jnp.einsum('nd,edf->nef', x, w_gate)) * jnp.einsum('nd,edf->nef', x, w_up)
    y = jnp.einsum('nef,efd->nd', hid * gates[:, :, None], w_down)
    return y.reshape(shp)

def setup_inputs(seed: int = 0) -> dict:
    key = jax.random.key(seed)
    ks = jax.random.split(key, 32)

    def nrm(i, shape, scale):
        return jax.random.normal(ks[i], shape, jnp.float32) * scale

    d = D_MODEL
    return {
        'x_prompt': nrm(0, (BATCH, SEQ, d), 1.0),
        'x_sample': nrm(1, (DEC_BATCH, DEC_SEQ, d), 1.0),
        'state_na_k': nrm(2, (DEC_BATCH, N_NA_LAYERS, PAST_LEN, NA_HEADS, NA_HEAD_DIM), 1.0),
        'state_na_v': nrm(3, (DEC_BATCH, N_NA_LAYERS, PAST_LEN, NA_HEADS, NA_HEAD_DIM), 1.0),
        'state_mla_ckv': nrm(4, (DEC_BATCH, N_MLA_LAYERS, PAST_LEN, MLA_KV_RANK), 1.0),
        'state_mla_kr': nrm(5, (DEC_BATCH, N_MLA_LAYERS, PAST_LEN, MLA_ROPE_DIM), 1.0),
        'c': nrm(6, (DEC_BATCH, d), 1.0),
        'c_ctx': nrm(7, (d,), 1.0),
        'ada_w': nrm(8, (DEPTH, d, N_MOD * d), d ** -0.5),
        'ada_b': nrm(9, (DEPTH, N_MOD * d), 0.02),
        'norm_mix_g': 1.0 + nrm(10, (DEPTH, d), 0.02),
        'norm_ffn_g': 1.0 + nrm(11, (DEPTH, d), 0.02),
        'final_norm_g': 1.0 + nrm(12, (d,), 0.02),
        'na_w_qkv': nrm(13, (N_NA_LAYERS, d, 3 * d), d ** -0.5),
        'na_w_o': nrm(14, (N_NA_LAYERS, d, d), d ** -0.5),
        'na_rpb': nrm(15, (N_NA_LAYERS, NA_HEADS, 2 * NA_KH - 1, 2 * NA_KW - 1), 0.1),
        'mla_w_in': nrm(16, (N_MLA_LAYERS, d, MLA_Q_RANK + MLA_KV_RANK + MLA_ROPE_DIM), d ** -0.5),
        'mla_q_norm_g': 1.0 + nrm(17, (N_MLA_LAYERS, MLA_Q_RANK), 0.02),
        'mla_kv_norm_g': 1.0 + nrm(18, (N_MLA_LAYERS, MLA_KV_RANK), 0.02),
        'mla_w_uq': nrm(19, (N_MLA_LAYERS, MLA_Q_RANK, MLA_HEADS * MLA_QK_DIM), MLA_Q_RANK ** -0.5),
        'mla_w_uk': nrm(20, (N_MLA_LAYERS, MLA_KV_RANK, MLA_HEADS * MLA_NOPE_DIM), MLA_KV_RANK ** -0.5),
        'mla_w_uv': nrm(21, (N_MLA_LAYERS, MLA_KV_RANK, MLA_HEADS * MLA_V_DIM), MLA_KV_RANK ** -0.5),
        'mla_w_o': nrm(22, (N_MLA_LAYERS, MLA_HEADS * MLA_V_DIM, d), (MLA_HEADS * MLA_V_DIM) ** -0.5),
        'moe_w_group': nrm(23, (DEPTH, d, N_GROUPS), d ** -0.5),
        'moe_b_group': nrm(24, (DEPTH, N_GROUPS), 0.01),
        'moe_w_expert': nrm(25, (DEPTH, d, N_EXPERTS), d ** -0.5),
        'moe_b_expert': nrm(26, (DEPTH, N_EXPERTS), 0.01),
        'moe_w_gate': nrm(27, (DEPTH, N_EXPERTS, d, D_FF_EXPERT), d ** -0.5),
        'moe_w_up': nrm(28, (DEPTH, N_EXPERTS, d, D_FF_EXPERT), d ** -0.5),
        'moe_w_down': nrm(29, (DEPTH, N_EXPERTS, D_FF_EXPERT, d), D_FF_EXPERT ** -0.5),
    }

def reference(x_prompt, x_sample, state_na_k, state_na_v, state_mla_ckv, state_mla_kr, c, c_ctx,
              ada_w, ada_b, norm_mix_g, norm_ffn_g, final_norm_g,
              na_w_qkv, na_w_o, na_rpb,
              mla_w_in, mla_q_norm_g, mla_kv_norm_g, mla_w_uq, mla_w_uk, mla_w_uv, mla_w_o,
              moe_w_group, moe_b_group, moe_w_expert, moe_b_expert, moe_w_gate, moe_w_up, moe_w_down):
    n_lat = x_sample.shape[1]
    rows = n_lat // GRID_W
    cos, sin = axial_rope_tables(n_lat)
    na_idx = na_window_indices(rows)
    xp, xs = x_prompt, x_sample
    na_k_out, na_v_out, ckv_out, kr_out = [], [], [], []
    for i in range(DEPTH):
        mod_p = ada_params(c_ctx, ada_w[i], ada_b[i])
        mod_s = ada_params(c, ada_w[i], ada_b[i])
        hp = modulate(rms_norm(xp, norm_mix_g[i]), mod_p[0], mod_p[1])
        hs = modulate(rms_norm(xs, norm_mix_g[i]), mod_s[0], mod_s[1])
        j = i // N_MIXERS
        if i % N_MIXERS == 0:
            yp, k_ctx, v_ctx = na_context(hp, na_w_qkv[j], na_w_o[j])
            ys = na_latent(hs, state_na_k[:, j], state_na_v[:, j], na_w_qkv[j], na_rpb[j], na_w_o[j], na_idx)
            na_k_out.append(k_ctx)
            na_v_out.append(v_ctx)
        else:
            mla_w = (mla_w_in[j], mla_q_norm_g[j], mla_kv_norm_g[j], mla_w_uq[j],
                     mla_w_uk[j], mla_w_uv[j], mla_w_o[j])
            yp, ckv_ctx, kr_ctx = mla_context(hp, *mla_w)
            ys = mla_latent(hs, state_mla_ckv[:, j], state_mla_kr[:, j], cos, sin, *mla_w)
            ckv_out.append(ckv_ctx)
            kr_out.append(kr_ctx)
        xp = xp + mod_p[2] * yp
        xs = xs + mod_s[2] * ys
        moe_w = (moe_w_group[i], moe_b_group[i], moe_w_expert[i], moe_b_expert[i],
                 moe_w_gate[i], moe_w_up[i], moe_w_down[i])
        hp = modulate(rms_norm(xp, norm_ffn_g[i]), mod_p[3], mod_p[4])
        hs = modulate(rms_norm(xs, norm_ffn_g[i]), mod_s[3], mod_s[4])
        xp = xp + mod_p[5] * hier_moe(hp, *moe_w)
        xs = xs + mod_s[5] * hier_moe(hs, *moe_w)
    y_prompt = rms_norm(xp, final_norm_g)
    y_sample = rms_norm(xs, final_norm_g)
    new_na_k = jnp.stack(na_k_out, axis=1)
    new_na_v = jnp.stack(na_v_out, axis=1)
    new_mla_ckv = jnp.stack(ckv_out, axis=1)
    new_mla_kr = jnp.stack(kr_out, axis=1)
    return (y_prompt, y_sample, new_na_k, new_na_v, new_mla_ckv, new_mla_kr)


_drawn_inputs = setup_inputs


def setup_inputs(seed=0):
    import zlib

    import numpy as np

    out = dict(_drawn_inputs(seed))
    spreads = {}
    factors = {'final_norm_g': 2.863,
     'mla_q_norm_g': 7.188,
     'mla_kv_norm_g': 2.742,
     'moe_b_expert': 4.652}
    for name, (base, spread) in spreads.items():
        noise = np.random.default_rng([zlib.crc32(name.encode()), seed]).standard_normal(out[name].shape)
        drawn = base * np.exp(spread * noise) if base else spread * noise
        out[name] = jnp.asarray(drawn.astype(out[name].dtype))
    for name, factor in factors.items():
        out[name] = (out[name] * factor).astype(out[name].dtype)
    return out
```

```python
from contextlib import ExitStack

import numpy as np

import concourse.bass as bass
from concourse import mybir

F32 = mybir.dt.float32
I32 = mybir.dt.int32
U32 = mybir.dt.uint32
ALU = mybir.AluOpType
ACT = mybir.ActivationFunctionType
AX_X = mybir.AxisListType.X

P = 128
D = 1024
KC = D // P
NL = 512
NC_ = 128
NT = NL + NC_
TT = NT // P
GRID_W, ROWS, QB = 64, 8, 16
NA_H, NA_DH = 16, 64
PAIRS = 8
NA_SCALE = NA_DH ** -0.5
QR, KVR, ROPE = 384, 256, 32
MLA_SCALE = 96.0 ** -0.5
KEYS = NT + P
NG, NE, EG = 4, 16, 4
FF = 256
SLOT = 128
NJOB = (2 * NT + NE * (SLOT - 1)) // SLOT
NPAIR = (NJOB + 1) // 2
NROWS = (2 * NPAIR + 2) * SLOT
EPS = 1e-6
BIG = 1e30
LOW = -3e38


class Buffers:
    pass


def spans():
    return ((0, NL, 0), (NL, NT, 1))


class Chain:

    def __init__(self, eng, sem):
        self.eng, self.sem, self.n = eng, sem, 0

    def step(self, ins):
        self.n += 1
        ins.then_inc(self.sem, 1)
        self.eng.wait_ge(self.sem, self.n)


def declare(nc, ctx):
    g = Buffers()

    def sb(name, shape, dt=F32):
        return ctx.enter_context(nc.sbuf_tensor(name, shape, dt))

    g.xT = sb("xT", [P, KC, NT])
    g.hT = sb("hT", [P, KC, NT])
    g.oT = sb("oT", [P, KC, NT])
    g.wbig = sb("wbig", [P, KC, D])
    g.ident = sb("ident", [P, P])
    g.ones = sb("ones", [P, P])
    g.cols = sb("cols", [P, 2 * 48 + 5 * KC + 5])
    g.modc = sb("modc", [P, 2, 2, 48])
    g.acol = sb("acol", [P, 2, KC])
    g.cs = sb("cs", [P, KC, 32])
    g.eps = sb("eps", [P, 1])
    g.rw = sb("rw", [P, 2, KC, NG + NE])
    g.rb = sb("rb", [1, 2, NG + NE])
    g.rowsb = sb("rowsb", [P, 512])
    g.bank = [ctx.enter_context(nc.psum_tensor(f"slot{s}", [P, 2, 512], F32)) for s in range(2)]
    g.pt = ctx.enter_context(nc.psum_tensor("pt", [P, 2, 512], F32))
    g.pb6 = ctx.enter_context(nc.psum_tensor("pb6", [P, 512], F32))
    g.pb7 = ctx.enter_context(nc.psum_tensor("pb7", [P, 512], F32))
    g.xs_rows = nc.dram_tensor("xs_rows", [NROWS, D], F32)
    g.bias_rows = nc.dram_tensor("bias_rows", [QB, NA_H, 15, 48], F32)
    g.bias_full = nc.dram_tensor("bias_full", [ROWS, QB, NA_H, ROWS * 48], F32)
    sem = lambda name: ctx.enter_context(nc.semaphore(name))
    g.stage_sems = []

    def stage_sem(name):
        g.stage_sems.append(nc.alloc_semaphore(name=name))
        return g.stage_sems[-1]

    g.sem = stage_sem
    g.ada_ld = [sem(f"ada_ld{b}") for b in range(2)]
    g.ada_mm, g.ada_row, g.ada_t, g.ada_col = sem("ada_mm"), sem("ada_row"), sem("ada_t"), sem("ada_col")
    g.wbig_ld = sem("wbig_ld")
    g.zero_st = sem("zero_st")
    return g


def end_stage(nc, g):
    nc.clear_and_free_semaphores(g.stage_sems)
    g.stage_sems.clear()
    nc.all_engine_barrier()


def slot2(g, s):
    return g.bank[s][:, :, :].rearrange("p a b -> p (a b)")


def ada_load(eng, g, t, step, ring):
    if step >= 2:
        eng.wait_ge(g.ada_mm, step - 1)
    l, grp, k = step // 24, step // 8 % 3, step % 8
    eng.dma_start(ring[:, step % 2, :], t["ada_w"][l, grp, k]).then_inc(g.ada_ld[step % 2], 16)


def ada_matmul(pe, g, step, ring):
    if step % 8 == 0 and step > 0:
        pe.wait_ge(g.ada_col, step // 8)
    pe.wait_ge(g.ada_ld[step % 2], 16 * (step // 2 + 1))
    k = step % 8
    for j in range(4):
        mm = pe.matmul(g.pb7[32 * j:32 * j + 32, :], g.cs[:, k, :], ring[:, step % 2, 512 * j:512 * j + 512],
                       start=(k == 0), stop=(k == 7), tile_position=(0, 32 * j))
    mm.then_inc(g.ada_mm, 1)


def ada_rows(dve, g, grp):
    dve.wait_ge(g.ada_mm, 8 * (grp + 1))
    dve.tensor_copy(g.rowsb[:, :], g.pb7[:, :]).then_inc(g.ada_row, 1)


def ada_turn(pe, g, grp):
    pe.wait_ge(g.ada_row, grp + 1)
    pick = g.ident[:, :].rearrange("p (j r) -> p j r", r=32)[:, :, 0:2]
    for m in range(4):
        mm = pe.matmul(g.pb7[:, 8 * m:8 * m + 8], g.rowsb[:, P * m:P * m + P], pick, start=True, stop=True)
    mm.then_inc(g.ada_t, 1)


def ada_columns(dve, g, grp):
    dve.wait_ge(g.ada_t, grp + 1)
    l, at = grp // 3, 16 * (grp % 3)
    got = g.pb7[:, 0:32].rearrange("p (m j c) -> p c j m", j=4, c=2)
    for c in range(2):
        ins = dve.tensor_tensor(g.modc[:, l, c, at:at + 16].rearrange("p (j m) -> p j m", m=4), got[:, c, :, :],
                                g.cols[:, 48 * l + at:48 * l + at + 16].rearrange("p (j m) -> p j m", m=4), ALU.add)
    ins.then_inc(g.ada_col, 1)


def stat_matmul(pe, g, sq, k, last, names):
    pe.wait_ge(names.sq, k + 1)
    pe.matmul(g.pt[:, 0, :], g.ones[:, :], sq[:, k % 2, 0:NL], start=(k == 0), stop=(k == last))
    pe.matmul(g.pt[:, 1, 0:NC_], g.ones[:, :], sq[:, k % 2, NL:NT], start=(k == 0), stop=(k == last))\
        .then_inc(names.st, 1)


def square(act, g, sq, k, src, names):
    if k >= 2:
        act.wait_ge(names.st, k - 1)
    act.activation(sq[:, k % 2, :], src, ACT.Square).then_inc(names.sq, 1)


def root(act, g, root_t, names):
    act.wait_ge(names.st, KC)
    flat = g.pt[:, :, :].rearrange("p a b -> p (a b)")
    act.activation(root_t[:, :], flat[:, 0:NT], ACT.Sqrt, bias=g.eps[:, 0:1], scale=1.0 / D).then_inc(names.root, 1)


def norm_sems(g, tag):
    n = Buffers()
    n.sq, n.st, n.root, n.rstd = (g.sem(f"{k}_{tag}") for k in ("sq", "st", "root", "rstd"))
    n.mul, n.aff, n.affp, n.a = (g.sem(f"{k}_{tag}") for k in ("mul", "aff", "affp", "a"))
    return n


def apply_dve(dve, g, root_t, rstd, names, l, which):
    dve.wait_ge(names.root, 1)
    dve.reciprocal(rstd[:, :], root_t[:, :]).then_inc(names.rstd, 1)
    if which is not None:
        gain = g.cols[:, 96 + KC * (2 * l + which):96 + KC * (2 * l + which) + KC]
        for c in range(2):
            dve.scalar_tensor_tensor(out=g.acol[:, c, :], in0=g.modc[:, l, c, 24 * which + 8:24 * which + 16],
                                     scalar=1.0, in1=gain, op0=ALU.add, op1=ALU.mult).then_inc(names.a, 1)
    dve.wait_ge(names.rstd, 1)
    for k in range(KC):
        dve.tensor_tensor(g.hT[:, k, :], g.xT[:, k, :], rstd[:, :], ALU.mult).then_inc(names.mul, 1)


def apply_act(act, g, names, l, which):
    act.wait_ge(names.a, 2)
    for k in range(KC):
        act.wait_ge(names.mul, k + 1)
        act.activation(g.hT[:, k, 0:NL], g.hT[:, k, 0:NL], ACT.Identity,
                       bias=g.modc[:, l, 0, 24 * which + k:24 * which + k + 1],
                       scale=g.acol[:, 0, k:k + 1]).then_inc(names.aff, 1)


def apply_pool(pool, g, names, l, which):
    pool.wait_ge(names.a, 2)
    for k in range(KC):
        pool.wait_ge(names.mul, k + 1)
        pool.tensor_scalar(g.hT[:, k, NL:NT], g.hT[:, k, NL:NT], g.acol[:, 1, k:k + 1],
                           g.modc[:, l, 1, 24 * which + k:24 * which + k + 1], ALU.mult, ALU.add)\
            .then_inc(names.affp, 1)


def stage_begin(nc, g, t):
    with ExitStack() as ctx:
        sb = lambda name, shape, dt=F32: ctx.enter_context(nc.sbuf_tensor(name, shape, dt))
        ring = g.ring
        sq = sb("b_sq", [P, 2, NT])
        root_t = sb("b_root", [P, NT])
        rstd = sb("b_rstd", [P, NT])
        c2 = sb("b_c2", [P, KC, 2])
        sg = sb("b_sg", [P, KC, 2])
        n = norm_sems(g, "b")
        x_ld, c_ld, cst_ld, z, sil, csr = (g.sem(f"b_{k}") for k in ("x_ld", "c_ld", "cst_ld", "z", "sil", "csr"))
        ep = g.sem("b_ep")
        block = ctx.enter_context(nc.Block())

        @block.sync
        def _(sp):
            sp.dma_start(c2[:, :, :], t["c2"]).then_inc(c_ld, 16)
            sp.dma_start(g.xT[:, :, :], t["xT"]).then_inc(x_ld, 16)
            for step in range(8):
                ada_load(sp, g, t, step, ring)
            sp.dma_start(g.wbig[:, :, :], t["na_wv"]).then_inc(g.wbig_ld, 16)

        @block.gpsimd
        def _(pool):
            pool.memset(g.cs[:, :, :], 0.0).then_inc(z, 1)
            pool.memset(g.ones[:, :], 1.0).then_inc(z, 1)
            pool.memset(g.eps[:, :], EPS).then_inc(z, 1)
            apply_pool(pool, g, n, 0, 0)

        @block.scalar
        def _(act):
            act.dma_start(g.ident[:, :], t["ident"]).then_inc(cst_ld, 16)
            act.dma_start(g.cols[:, :], t["cols"]).then_inc(cst_ld, 16)
            act.dma_start(g.rw[:, :, :, :], t["rw"]).then_inc(cst_ld, 16)
            act.dma_start(g.rb[:, :, :], t["rb"]).then_inc(cst_ld, 16)
            act.wait_ge(c_ld, 16)
            act.activation(sg[:, :, :], c2[:, :, :], ACT.Silu).then_inc(sil, 1)
            act.wait_ge(x_ld, 16)
            for k in range(KC):
                square(act, g, sq, k, g.xT[:, k, :], n)
            act.wait_ge(z, 3)
            root(act, g, root_t, n)
            apply_act(act, g, n, 0, 0)

        @block.tensor
        def _(pe):
            pe.wait_ge(z, 3)
            for k in range(KC):
                stat_matmul(pe, g, sq, k, KC - 1, n)
            pe.wait_ge(csr, 1)
            pe.wait_ge(cst_ld, 64)
            for step in range(8):
                ada_matmul(pe, g, step, ring)
            ada_turn(pe, g, 0)

        @block.vector
        def _(dve):
            dve.wait_ge(z, 3)
            dve.wait_ge(sil, 1)
            dve.tensor_copy(g.cs[:, :, 0:2], sg[:, :, :]).then_inc(csr, 1)
            ada_rows(dve, g, 0)
            dve.wait_ge(cst_ld, 64)
            ada_columns(dve, g, 0)
            dve.wait_ge(g.ada_col, 1)
            dve.wait_ge(x_ld, 16)
            apply_dve(dve, g, root_t, rstd, n, 0, 0)


def stage_na(nc, g, t):
    with ExitStack() as ctx:
        sb = lambda name, shape, dt=F32: ctx.enter_context(nc.sbuf_tensor(name, shape, dt))
        sem = lambda name: g.sem("n_" + name)
        ring = g.ring
        V = sb("n_V", [P, TT + 1, D])
        wqk = sb("n_wqk", [P, 3, KC, P])
        qT = sb("n_qT", [P, 2, NT])
        kT = sb("n_kT", [P, 2, NT])
        kcT = sb("n_kcT", [P, PAIRS, P])
        S = sb("n_S", [P, 3, 2, 512])
        PT = sb("n_PT", [P, 2, 2, 512])
        NBH = 3
        nb_int = sb("n_nbi", [P, NBH, 512])
        nb_edge = sb("n_nbe", [P, NBH, 640])
        braw = sb("n_braw", [P, 2, ROWS, 3, QB])
        mask = sb("n_mask", [P, 3, P])
        mask_e = sb("n_maske", [P, 2, P])
        st = sb("n_st", [P, 3, 2, 3])
        v_ld, kc_ld, wv_done = sem("v_ld"), sem("kc_ld"), sem("wv_done")
        w_ld = [sem(f"w_ld{b}") for b in range(3)]
        front, q_rdy, k_rdy, v_rdy = sem("front"), sem("q_rdy"), sem("k_rdy"), sem("v_rdy")
        free = [sem(f"free{s}") for s in range(2)]
        br_ld = [sem(f"br_ld{b}") for b in range(2)]
        b3 = sem("b3")
        b2, m_ld, nbz, nb_rdy = sem("b2"), sem("m_ld"), sem("nbz"), sem("nb_rdy")
        ttr, ex, rcp, prob, tr = sem("ttr"), sem("ex"), sem("rcp"), sem("prob"), sem("tr")
        pta, ptd, pv, oev = sem("pta"), sem("ptd"), sem("pv"), sem("oev")
        out_st = sem("out_st")
        kout = [sem(f"kout{b}") for b in range(2)]

        units = [("v", i) for i in range(TT)] + [("q", 0), ("k", 0)]
        for p in range(PAIRS):
            units += [("s", p, 0), ("s", p, 1)]
            if p + 1 < PAIRS:
                units += [("q", p + 1), ("k", p + 1)]
            units += [("s", p, 2), ("s", p, 3), ("s", p, 4)]
        NA = 5 * PAIRS
        unit_of = [units.index((w, p)) for p in range(PAIRS) for w in "qk"]

        def window(n):
            return (4, 4) if n == 4 else (max(0, n - 1), min(3, n + 1))

        def vtiles(n):
            lo, hi = window(n)
            return list(range(lo, hi + 1)) + ([TT] if n < 4 else [])

        block = ctx.enter_context(nc.Block())

        @block.sync
        def _(sp):
            def load_w(j):
                if j >= 3:
                    sp.wait_ge(front, unit_of[j - 3] + 1)
                sp.dma_start(wqk[:, j % 3, :, :], t["na_wqk"][j]).then_inc(w_ld[j % 3], 16)
            load_w(0)
            load_w(1)
            sp.dma_start(kcT[:, :, :], t["na_kcT"]).then_inc(kc_ld, 16)
            sp.dma_start(V[:, TT, :], t["na_vc"]).then_inc(v_ld, 16)
            load_w(2)
            for p in range(PAIRS):
                for j in range(2 * p + 3, min(2 * p + 5, 2 * PAIRS)):
                    load_w(j)
                for a in range(5 * p, 5 * p + 5):
                    ada_load(sp, g, t, 8 + a, ring)
                if p == 0:
                    sp.wait_ge(wv_done, TT)
                    sp.dma_start(g.wbig[:, :, :], t["na_wo"]).then_inc(g.wbig_ld, 16)
                    sp.wait_ge(v_rdy, TT)
                    sp.dma_start(t["new_v"], V[:, TT - 1, :]).then_inc(out_st, 16)
            sp.wait_ge(out_st, 16)

        @block.gpsimd
        def _(pool):
            for c in range(QB):
                pool.dma_start(g.bias_rows[c].rearrange("h y x -> (h y) x"), t["rpb"][:, 15 - c:63 - c]).then_inc(b2, 16)
            pool.dma_start(mask[:, :, :], t["mask"]).then_inc(m_ld, 16)
            pool.dma_start(mask_e[:, :, :], t["mask_e"]).then_inc(m_ld, 16)
            pool.memset(nb_int[:, :, 384:512], 0.0).then_inc(nbz, 1)
            pool.memset(nb_edge[:, :, 256:384], 0.0).then_inc(nbz, 1)
            pool.wait_ge(b2, 16 * QB)
            for r in range(ROWS):
                pool.dma_start(g.bias_full[r], g.bias_rows[:, :, 7 - r:15 - r, :].rearrange("c h y x -> c h (y x)"))\
                    .then_inc(b3, 16)
            pool.wait_ge(b3, 16 * ROWS)

            def load_bias(h):
                if h >= 2:
                    pool.wait_ge(nb_rdy, 7 * (h - 1))
                pool.dma_start(braw[:, h % 2, :, :, :].rearrange("p a b c -> p (a b c)"),
                               g.bias_full[:, :, h, :].rearrange("r c x -> (r c) x"))\
                    .then_inc(br_ld[h % 2], 16)

            def prepare(h):
                pool.wait_ge(br_ld[h % 2], 16 * (h // 2 + 1))
                if h >= NBH:
                    pool.wait_ge(ttr, 5 * ((h - NBH) // 2 + 1))
                rel = lambda m: braw[:, h % 2, :, m, :]
                out3 = lambda ap: ap.rearrange("p (a b) -> p a b", a=ROWS)
                m3 = lambda ap: ap.rearrange("p (a b) -> p a b", a=ROWS)
                b = h % NBH
                for m in range(3):
                    pool.tensor_tensor(out3(nb_int[:, b, P * m:P * m + P]), m3(mask[:, m, :]), rel(m), ALU.subtract)\
                        .then_inc(nb_rdy, 1)
                pool.tensor_tensor(out3(nb_edge[:, b, 0:P]), m3(mask_e[:, 0, :]), rel(1), ALU.subtract).then_inc(nb_rdy, 1)
                pool.tensor_tensor(out3(nb_edge[:, b, P:2 * P]), m3(mask[:, 2, :]), rel(2), ALU.subtract).then_inc(nb_rdy, 1)
                pool.tensor_tensor(out3(nb_edge[:, b, 384:512]), m3(mask[:, 0, :]), rel(0), ALU.subtract).then_inc(nb_rdy, 1)
                pool.tensor_tensor(out3(nb_edge[:, b, 512:640]), m3(mask_e[:, 1, :]), rel(1), ALU.subtract).then_inc(nb_rdy, 1)

            load_bias(0)
            load_bias(1)
            pool.wait_ge(m_ld, 32)
            prepare(0)
            load_bias(2)
            prepare(1)
            load_bias(3)
            pool.memset(g.zero[:, :], 0.0).then_inc(nbz, 1)
            pool.wait_ge(nbz, 3)
            for r in range(NROWS // P):
                pool.dma_start(g.xs_rows[r * P:r * P + P, :].rearrange("p (a b) -> p a b", b=256),
                               g.zero[:, :].unsqueeze(1).broadcast_to([P, 4, 256])).then_inc(g.zero_st, 16)

            for a in range(NA):
                p = a // 5
                if a % 5 == 4 and 2 * p + 3 < NA_H:
                    prepare(2 * p + 3)
                    if 2 * p + 5 < NA_H:
                        load_bias(2 * p + 5)
                if a % 5 == 0 and 2 * p + 2 < NA_H:
                    prepare(2 * p + 2)
                    if 2 * p + 4 < NA_H:
                        load_bias(2 * p + 4)

        @block.tensor
        def _(pe):
            def slot_free(u):
                if u >= 2:
                    pe.wait_ge(free[u % 2], u // 2)

            def project(u, j):
                slot_free(u)
                pe.wait_ge(w_ld[j % 3], 16 * (j // 3 + 1))
                for lo, hi, c in spans():
                    for k in range(KC):
                        mm = pe.matmul(g.bank[u % 2][:, c, 0:hi - lo], wqk[:, j % 3, k, :], g.hT[:, k, lo:hi],
                                       start=(k == 0), stop=(k == KC - 1))
                mm.then_inc(front, 1)

            def values(u, i):
                slot_free(u)
                pe.wait_ge(g.wbig_ld, 16)
                for half in range(2):
                    for k in range(KC):
                        mm = pe.matmul(g.bank[u % 2][:, half, :], g.hT[:, k, P * i:P * i + P],
                                       g.wbig[:, k, 512 * half:512 * half + 512], start=(k == 0), stop=(k == KC - 1))
                mm.then_inc(front, 1)

            def scores(u, p, n):
                slot_free(u)
                pe.wait_ge(q_rdy, p + 1)
                pe.wait_ge(k_rdy, p + 1)
                pe.wait_ge(kc_ld, 16)
                lo, hi = window(n)
                w = P * (hi - lo + 1)
                for h in range(2):
                    rows = slice(64 * h, 64 * h + 64)
                    at = P if n == 3 else 0
                    mm = pe.matmul(g.bank[u % 2][:, h, at:at + w],
                                   qT[rows, p % 2, P * n:P * n + P], kT[rows, p % 2, P * lo:P * lo + w],
                                   start=True, stop=True)
                    if n < 4:
                        at = 0 if n == 3 else w
                        mm = pe.matmul(g.bank[u % 2][:, h, at:at + P], qT[rows, p % 2, P * n:P * n + P],
                                       kcT[rows, p, :], start=True, stop=True)
                mm.then_inc(front, 1)

            def turn(a):
                pe.wait_ge(prob, a + 1)
                if a >= 1:
                    pe.wait_ge(pta, a)
                    pe.wait_ge(ptd, a)
                for h in range(2):
                    for i in range(len(vtiles(a % 5))):
                        mm = pe.transpose(g.pt[:, h, P * i:P * i + P], S[:, a % 3, h, P * i:P * i + P], g.ident[:, :])
                mm.then_inc(tr, 1)

            def weigh(a):
                p, n = a // 5, a % 5
                pe.wait_ge(pta, a + 1)
                pe.wait_ge(ptd, a + 1)
                if a >= 1:
                    pe.wait_ge(oev, a)
                tiles = vtiles(n)
                if n == 3:
                    tiles = [TT] + tiles[:-1]
                for i, vt in enumerate(tiles):
                    for h in range(2):
                        mm = pe.matmul(g.pb6[64 * h:64 * h + 64, 0:P],
                                       V[:, vt, P * p + 64 * h:P * p + 64 * h + 64], PT[:, a % 2, h, P * i:P * i + P],
                                       start=(i == 0), stop=(i == len(tiles) - 1), tile_position=(0, 64 * h))
                mm.then_inc(pv, 1)

            a = 0
            for u, unit in enumerate(units):
                if unit[0] == "v":
                    values(u, unit[1])
                elif unit[0] == "s":
                    scores(u, unit[1], unit[2])
                    if a == 0:
                        pe.wait_ge(v_rdy, TT)
                        pe.wait_ge(v_ld, 16)
                    if a >= 2:
                        turn(a - 2)
                    if a >= 3:
                        weigh(a - 3)
                    if a > 0 and a % 8 == 0:
                        ada_turn(pe, g, a // 8)
                    ada_matmul(pe, g, 8 + a, ring)
                    a += 1
                else:
                    project(u, 2 * unit[1] + (unit[0] == "k"))
            turn(NA - 2)
            weigh(NA - 3)
            turn(NA - 1)
            weigh(NA - 2)
            weigh(NA - 1)
            ada_turn(pe, g, 5)

        @block.vector
        def _(dve):
            def reciprocals(a):
                dve.wait_ge(ex, 2 * (a + 1))
                dve.reciprocal(st[:, a % 3, :, 2:3], st[:, a % 3, :, 1:2]).then_inc(rcp, 1)
                dve.wait_ge(rcp, a + 1)
                w = P * len(vtiles(a % 5))
                for h in range(2):
                    ins = dve.tensor_scalar(S[:, a % 3, h, 0:w], S[:, a % 3, h, 0:w], st[:, a % 3, h, 2:3], None, ALU.mult)
                ins.then_inc(prob, 1)

            def evacuate(a):
                dve.wait_ge(tr, a + 1)
                if a >= 2:
                    dve.wait_ge(pv, a - 1)
                w = P * len(vtiles(a % 5))
                dve.tensor_copy(PT[:, a % 2, 1, 0:w], g.pt[:, 1, 0:w]).then_inc(ptd, 1)

            a = 0
            for u, unit in enumerate(units):
                if unit[0] == "v":
                    dve.wait_ge(front, u + 1)
                    dve.tensor_copy(V[:, unit[1], :], slot2(g, u % 2)).then_inc(free[u % 2], 1)
                    dve.wait_ge(free[u % 2], u // 2 + 1)
                    dve.sem_inc(v_rdy, 1)
                    dve.sem_inc(wv_done, 1)
                elif unit[0] == "k":
                    dve.wait_ge(front, u + 1)
                    if unit[1] >= 2:
                        dve.wait_ge(kout[unit[1] % 2], 16 * (unit[1] // 2))
                    dve.tensor_copy(kT[:, unit[1] % 2, :], slot2(g, u % 2)[:, 0:NT]).then_inc(free[u % 2], 1)
                    dve.wait_ge(free[u % 2], u // 2 + 1)
                    dve.sem_inc(k_rdy, 1)
                elif unit[0] == "s":
                    p, n = unit[1:]
                    dve.wait_ge(front, u + 1)
                    dve.wait_ge(nb_rdy, 14 * (p + 1))
                    dve.wait_ge(nbz, 2)
                    if a >= 3:
                        dve.wait_ge(tr, a - 2)
                    w = P * len(vtiles(n))
                    for h in range(2):
                        b = (2 * p + h) % NBH
                        nbias = {0: nb_edge[:, b, 0:384], 1: nb_int[:, b, :], 2: nb_int[:, b, :],
                                 3: nb_edge[:, b, 256:640], 4: nb_edge[:, b, 256:384]}[n]
                        ins = dve.tensor_tensor_reduce(S[:, a % 3, h, 0:w], g.bank[u % 2][:, h, 0:w], nbias, 1.0, 3e38,
                                                       ALU.add, ALU.min, st[:, a % 3, h, 0:1])
                    ins.then_inc(free[u % 2], 1)
                    dve.wait_ge(free[u % 2], u // 2 + 1)
                    dve.sem_inc(ttr, 1)
                    if a > 0 and a % 8 == 0:
                        ada_rows(dve, g, a // 8)
                        ada_columns(dve, g, a // 8)
                    if a >= 1:
                        reciprocals(a - 1)
                    if a >= 2:
                        evacuate(a - 2)
                    a += 1
            reciprocals(NA - 1)
            evacuate(NA - 2)
            evacuate(NA - 1)
            ada_rows(dve, g, 5)
            ada_columns(dve, g, 5)

        @block.scalar
        def _(act):
            def evacuate(a):
                act.wait_ge(tr, a + 1)
                if a >= 2:
                    act.wait_ge(pv, a - 1)
                w = P * len(vtiles(a % 5))
                act.activation(PT[:, a % 2, 0, 0:w], g.pt[:, 0, 0:w], ACT.Copy).then_inc(pta, 1)

            def outputs(a):
                act.wait_ge(pv, a + 1)
                p, n = a // 5, a % 5
                act.activation(g.oT[:, p, P * n:P * n + P], g.pb6[:, 0:P], ACT.Copy).then_inc(oev, 1)

            a = 0
            for u, unit in enumerate(units):
                if unit[0] == "q":
                    act.wait_ge(front, u + 1)
                    act.activation(qT[:, unit[1] % 2, :], slot2(g, u % 2)[:, 0:NT], ACT.Copy, scale=-NA_SCALE)\
                        .then_inc(free[u % 2], 1)
                    act.wait_ge(free[u % 2], u // 2 + 1)
                    act.sem_inc(q_rdy, 1)
                elif unit[0] == "s":
                    p, n = unit[1:]
                    act.wait_ge(ttr, a + 1)
                    w = P * len(vtiles(n))
                    for h in range(2):
                        act.activation(S[:, a % 3, h, 0:w], S[:, a % 3, h, 0:w], ACT.Exp, bias=st[:, a % 3, h, 0:1],
                                       scale=-1.0, accum_out=st[:, a % 3, h, 1:2]).then_inc(ex, 1)
                    if n == 0:
                        act.wait_ge(k_rdy, p + 1)
                        act.dma_start(t["new_kT"][p], kT[:, p % 2, NL:NT]).then_inc(kout[p % 2], 16)
                    if a >= 2:
                        evacuate(a - 2)
                    if a >= 3:
                        outputs(a - 3)
                    a += 1
            evacuate(NA - 2)
            outputs(NA - 3)
            evacuate(NA - 1)
            outputs(NA - 2)
            outputs(NA - 1)
            for b in range(2):
                act.wait_ge(kout[b], 16 * PAIRS // 2)


def stage_out(nc, g, t, l):
    with ExitStack() as ctx:
        sb = lambda name, shape, dt=F32: ctx.enter_context(nc.sbuf_tensor(f"o{l}_{name}", shape, dt))
        sem = lambda name: g.sem(f"o{l}_{name}")
        sq, root_t, rstd = sb("sq", [P, 2, NT]), sb("root", [P, NT]), sb("rstd", [P, NT])
        n = norm_sems(g, f"o{l}")
        front, res = sem("front"), sem("res")
        block = ctx.enter_context(nc.Block())

        @block.tensor
        def _(pe):
            pe.wait_ge(g.wbig_ld, 32 if l == 0 else 64)
            for m in range(KC):
                if m >= 2:
                    pe.wait_ge(res, 2 * (m - 1))
                for lo, hi, c in spans():
                    for k in range(KC):
                        mm = pe.matmul(g.bank[m % 2][:, c, 0:hi - lo], g.wbig[:, k, P * m:P * m + P], g.oT[:, k, lo:hi],
                                       start=(k == 0), stop=(k == KC - 1))
                mm.then_inc(front, 1)
                if m >= 1:
                    stat_matmul(pe, g, sq, m - 1, KC - 1, n)
            stat_matmul(pe, g, sq, KC - 1, KC - 1, n)

        @block.vector
        def _(dve):
            for m in range(KC):
                dve.wait_ge(front, m + 1)
                for lo, hi, c in spans():
                    dve.scalar_tensor_tensor(out=g.xT[:, m, lo:hi], in0=g.bank[m % 2][:, c, 0:hi - lo],
                                             scalar=g.modc[:, l, c, 16 + m:17 + m], in1=g.xT[:, m, lo:hi],
                                             op0=ALU.mult, op1=ALU.add).then_inc(res, 1)
            apply_dve(dve, g, root_t, rstd, n, l, 1)

        @block.scalar
        def _(act):
            for m in range(KC):
                act.wait_ge(res, 2 * (m + 1))
                square(act, g, sq, m, g.xT[:, m, :], n)
            root(act, g, root_t, n)
            apply_act(act, g, n, l, 1)

        @block.gpsimd
        def _(pool):
            apply_pool(pool, g, n, l, 1)


def stage_route(nc, g, t, l, m):
    with ExitStack() as ctx:
        sb = lambda name, shape, dt=F32: ctx.enter_context(nc.sbuf_tensor(f"r{l}_{name}", shape, dt))
        sem = lambda name: g.sem(f"r{l}_{name}")
        hrow = sb("hrow", [P, TT, D])
        lg = sb("lg", [P, TT, NG + NE])
        g8, gm, gi = sb("g8", [P, TT, 8]), sb("gm", [P, TT, 8]), sb("gi", [P, TT, 8], U32)
        gidx, ohg, d4, pen = sb("gidx", [P, TT, 1]), sb("ohg", [P, TT, NG]), sb("d4", [P, TT, NG]), sb("pen", [P, TT, NG])
        pg = sb("pg", [P, TT, 1])
        c16, em, ei = sb("c16", [P, TT, NE]), sb("em", [P, TT, 8]), sb("ei", [P, TT, 8], U32)
        eidx, e2 = sb("eidx", [P, TT, 2]), sb("e2", [P, TT, 1])
        oh, mask, prod = sb("oh", [P, 2, TT, NE]), sb("mask", [P, TT, NE]), sb("prod", [P, TT, NE])
        pos, slotf = sb("pos", [P, TT, NE]), sb("slotf", [P, 2, TT, 1])
        cst = sb("cst", [P, 3 * P])
        iota, tri, tri16 = cst[:, 0:32], cst[:, P:2 * P], cst[:, 2 * P:2 * P + 32]
        thr = cst[0:NE, 32:37]
        cmp5, ncnt, nb = sb("cmp5", [NE, 5]), sb("ncnt", [NE, 1]), sb("nb", [NE, P])
        ends, cmpj, jf, jp = sb("ends", [NE, 1]), sb("cmpj", [NE, 32]), sb("jf", [1, 34]), sb("jp", [1, 16])
        tot = sb("tot", [1, 1])
        c_ld, lgs, trs, evs, ex, ch = (sem(k) for k in ("c_ld", "lgs", "trs", "evs", "ex", "ch"))
        dd, msk, cnt, nbr, posr, endr, ejr, sl, sc = (sem(k) for k in ("dd", "msk", "cnt", "nbr", "posr", "endr", "ejr", "sl", "sc"))
        evb = [sem(f"evb{i}") for i in range(2)]
        nrd, enr = sem("nrd"), sem("enr")
        block = ctx.enter_context(nc.Block())

        @block.sync
        def _(sp):
            sp.dma_start(cst[:, :], t["cst"]).then_inc(c_ld, 16)

        @block.tensor
        def _(pe):
            for i in range(TT):
                o = g.pb6[:, 32 * i:32 * i + NG + NE]
                for k in range(KC):
                    pe.matmul(o, g.hT[:, k, P * i:P * i + P], g.rw[:, l, k, :], start=(k == 0), stop=False)
                mm = pe.matmul(o, g.ones[0:1, 0:P], g.rb[0:1, l, :], start=False, stop=True)
            mm.then_inc(lgs, 1)
            for i in range(TT):
                for half in range(2):
                    j = 2 * i + half
                    if j >= 2:
                        pe.wait_ge(evb[j % 2], j // 2)
                    for q in range(4):
                        mm = pe.transpose(g.bank[j % 2][:, 0, P * q:P * q + P], g.hT[:, 4 * half + q, P * i:P * i + P],
                                          g.ident[:, :])
                    mm.then_inc(trs, 1)
            pe.wait_ge(msk, 1)
            for i in range(TT):
                mm = pe.matmul(g.pb7[0:NE, 0:1], mask[:, i, :], g.ones[:, 0:1], start=(i == 0), stop=(i == TT - 1))
            mm.then_inc(cnt, 1)
            pe.wait_ge(nbr, 1)
            for i in range(TT):
                o = g.pt[:, 0, NE * i:NE * i + NE]
                pe.matmul(o, tri, mask[:, i, :], start=True, stop=False)
                for j in range(i):
                    pe.matmul(o, g.ones[:, :], mask[:, j, :], start=False, stop=False)
                mm = pe.matmul(o, nb[:, :], tri16[0:NE, 0:NE], start=False, stop=True)
            mm.then_inc(posr, 1)
            pe.wait_ge(nrd, 1)
            pe.matmul(g.pb7[0:NE, 0:1], tri16[0:NE, NE:2 * NE], ncnt[:, :], start=True, stop=True)
            pe.matmul(g.pb7[0:1, 4:5], ncnt[:, :], g.ones[0:NE, 0:1], start=True, stop=True).then_inc(endr, 1)
            pe.wait_ge(enr, 1)
            pe.matmul(g.pb6[0:1, 0:32], g.ones[0:NE, 0:1], cmpj[:, :], start=True, stop=True).then_inc(ejr, 1)

        @block.scalar
        def _(act):
            def evac(j):
                act.wait_ge(trs, j + 1)
                act.activation(hrow[:, j // 2, 512 * (j % 2):512 * (j % 2) + 512], g.bank[j % 2][:, 0, :], ACT.Copy)\
                    .then_inc(evb[j % 2], 1)
            for j in range(4):
                evac(j)
            act.wait_ge(dd, 1)
            act.activation(d4[:, :, :], d4[:, :, :], ACT.Exp).then_inc(ex, 1)
            for j in range(4, 2 * TT):
                evac(j)
            act.wait_ge(dd, 2)
            act.activation(e2[:, :, :], e2[:, :, :], ACT.Exp).then_inc(ex, 1)

        @block.vector
        def _(dve):
            c = Chain(dve, ch)
            dve.memset(g8[:, :, :], LOW)
            dve.wait_ge(c_ld, 16)
            dve.wait_ge(lgs, 1)
            c.step(dve.tensor_copy(lg[:, :, :], g.pb6[:, 0:32 * TT].rearrange("p (a b) -> p a b", b=32)[:, :, 0:NG + NE]))
            c.step(dve.tensor_copy(g8[:, :, 0:NG], lg[:, :, 0:NG]))
            for i in range(TT):
                last = dve.max(gm[:, i, :], g8[:, i, :])
            c.step(last)
            dve.tensor_tensor(d4[:, :, :], lg[:, :, 0:NG], gm[:, :, 0:1].broadcast_to([P, TT, NG]), ALU.subtract).then_inc(dd, 1)
            for i in range(TT):
                last = dve.max_index(gi[:, i, :], gm[:, i, :], g8[:, i, :])
            c.step(last)
            c.step(dve.tensor_copy(gidx[:, :, :], gi[:, :, 0:1]))
            c.step(dve.tensor_tensor(ohg[:, :, :], iota[:, 0:NG].unsqueeze(1).broadcast_to([P, TT, NG]),
                                     gidx[:, :, :].broadcast_to([P, TT, NG]), ALU.is_equal))
            c.step(dve.tensor_scalar(pen[:, :, :], ohg[:, :, :], -LOW, LOW, ALU.mult, ALU.add))
            c.step(dve.tensor_tensor(c16[:, :, :].rearrange("p t (a b) -> p t a b", b=EG),
                                     lg[:, :, NG:NG + NE].rearrange("p t (a b) -> p t a b", b=EG),
                                     pen[:, :, :].unsqueeze(3).broadcast_to([P, TT, NG, EG]), ALU.add))
            for i in range(TT):
                last = dve.max(em[:, i, :], c16[:, i, :])
            c.step(last)
            dve.tensor_tensor(e2[:, :, :], em[:, :, 1:2], em[:, :, 0:1], ALU.subtract).then_inc(dd, 1)
            for i in range(TT):
                last = dve.max_index(ei[:, i, :], em[:, i, :], c16[:, i, :])
            c.step(last)
            c.step(dve.tensor_copy(eidx[:, :, :], ei[:, :, 0:2]))
            for k in range(2):
                last = dve.tensor_tensor(oh[:, k, :, :], iota[:, 0:NE].unsqueeze(1).broadcast_to([P, TT, NE]),
                                         eidx[:, :, k:k + 1].broadcast_to([P, TT, NE]), ALU.is_equal)
            c.step(last)
            dve.tensor_tensor(mask[:, :, :], oh[:, 0, :, :], oh[:, 1, :, :], ALU.add).then_inc(msk, 1)
            dve.wait_ge(ex, 1)
            c.step(dve.reduce_sum(pg[:, :, :], d4[:, :, :], AX_X))
            c.step(dve.reciprocal(pg[:, :, :], pg[:, :, :]))
            dve.wait_ge(ex, 2)
            c.step(dve.tensor_scalar_add(m.w12[:, 0, :, :], e2[:, :, :], 1.0))
            c.step(dve.reciprocal(m.w12[:, 0, :, :], m.w12[:, 0, :, :]))
            c.step(dve.tensor_tensor(m.w12[:, 0, :, :], m.w12[:, 0, :, :], pg[:, :, :], ALU.mult))
            c.step(dve.tensor_tensor(m.w12[:, 1, :, :], m.w12[:, 0, :, :], e2[:, :, :], ALU.mult))
            dve.wait_ge(cnt, 1)
            c.step(dve.tensor_scalar(cmp5[:, :], thr, g.pb7[0:NE, 0:1], None, ALU.is_lt))
            dve.reduce_sum(ncnt[:, :], cmp5[:, :], AX_X).then_inc(nrd, 1)
            dve.wait_ge(nrd, 1)
            dve.tensor_scalar(nb[:, :], g.ones[0:NE, :], ncnt[:, 0:1], None, ALU.mult).then_inc(nbr, 1)
            dve.wait_ge(posr, 1)
            c.step(dve.tensor_copy(pos[:, :, :], g.pt[:, 0, 0:NE * TT].rearrange("p (a b) -> p a b", b=NE)))
            for k in range(2):
                c.step(dve.tensor_tensor(prod[:, :, :], pos[:, :, :], oh[:, k, :, :], ALU.mult))
                c.step(dve.reduce_sum(slotf[:, k, :, :], prod[:, :, :], AX_X))
            dve.tensor_copy(m.slot[:, :, :], slotf[:, :, :, :].rearrange("p k t o -> p k (t o)")).then_inc(sl, 1)
            dve.wait_ge(endr, 1)
            c.step(dve.tensor_copy(ends[:, :], g.pb7[0:NE, 0:1]))
            c.step(dve.tensor_copy(tot[:, :], g.pb7[0:1, 4:5]))
            dve.tensor_scalar(cmpj[:, :], iota[0:NE, :], ends[:, 0:1], None, ALU.is_ge).then_inc(enr, 1)
            c.step(dve.tensor_scalar(jp[:, :], cst[0:1, 40:56], tot[0:1, 0:1], None, ALU.is_lt))
            c.step(dve.reduce_sum(jf[:, 32:33], jp[:, 0:16], AX_X))
            dve.wait_ge(ejr, 1)
            c.step(dve.tensor_scalar(jf[:, 0:32], g.pb6[0:1, 0:32], float(NE - 1), None, ALU.min))
            c.step(dve.tensor_copy(m.jobs[:, 0:33], jf[:, 0:33]))

        @block.gpsimd
        def _(pool):
            pool.wait_ge(sl, 1)
            pool.wait_ge(evb[0], TT)
            pool.wait_ge(evb[1], TT)
            pool.wait_ge(g.zero_st, 16 * (NROWS // P))
            for i in range(TT):
                for k in range(2):
                    pool.indirect_dma_start(g.xs_rows[:, :], bass.IndirectOffsetOnAxis(m.slot[:, k, i:i + 1], 0),
                                            hrow[:, i, :], None).then_inc(sc, 16)
            pool.wait_ge(sc, 32 * TT)


def stage_experts(nc, g, t, l, m):
    with ExitStack() as ctx:
        sb = lambda name, shape, dt=F32: ctx.enter_context(nc.sbuf_tensor(f"e{l}_{name}", shape, dt))
        sem2 = lambda name: [g.sem(f"e{l}_{name}{b}") for b in range(2)]
        wg, wd = [sb(f"wg{b}", [P, KC, 2 * FF]) for b in range(2)], [sb(f"wd{b}", [P, 2, D]) for b in range(2)]
        xr = [sb(f"xr{b}", [P, D]) for b in range(2)]
        xg = [sb(f"xg{b}", [P, KC, P]) for b in range(2)]
        sg, hid, hT = ([sb(f"{k}{b}", [P, FF]) for b in range(2)] for k in ("sg", "hid", "hT"))
        y = [sb(f"y{b}", [P, D]) for b in range(2)]
        wg_ld, wd_ld, x_ld, tx, xga, xgd = (sem2(k) for k in ("wg_ld", "wd_ld", "x_ld", "tx", "xga", "xgd"))
        gu, sil, hd, th, hte, dn, ya, yd, y_st = (sem2(k) for k in ("gu", "sil", "hd", "th", "hte", "dn", "ya", "yd", "y_st"))
        block = ctx.enter_context(nc.Block())

        def count(eng):
            return eng.snap(eng.value_load(m.jobs[0:1, 32:33], min_val=1, max_val=NPAIR))

        @block.sync
        def _(sp):
            n = count(sp)
            for b in range(2):
                sp.dma_start(xr[b][:, :], g.xs_rows[P * b:P * b + P, :]).then_inc(x_ld[b], 16)
            with sp.Fori(0, NPAIR) as i:
                with sp.If(i < n):
                    e = [sp.snap(sp.value_load(m.jobs[0:1, bass.ds(2 * i + b, 1)], min_val=0, max_val=NE - 1)) for b in range(2)]
                    for b in range(2):
                        sp.wait_ge(gu[b], i + 1)
                        sp.dma_start(wg[b][:, :, :].rearrange("p a b -> p (a b)"), t["moe_gu"][l][e[b]]).then_inc(wg_ld[b], 16)
                    for b in range(2):
                        sp.wait_ge(dn[b], i + 1)
                        sp.dma_start(wd[b][:, :, :].rearrange("p a b -> p (a b)"), t["moe_dn"][l][e[b]]).then_inc(wd_ld[b], 16)
                        sp.wait_ge(tx[b], i + 1)
                        sp.dma_start(xr[b][:, :], g.xs_rows[bass.ds((2 * i + 2 + b) * P, P), :]).then_inc(x_ld[b], 16)

        @block.tensor
        def _(pe):
            n = count(pe)

            def turn_rows(b):
                for q in range(KC):
                    half = g.bank[0][:, q // 4, :]
                    mm = pe.transpose(half[:, P * (q % 4):P * (q % 4) + P], xr[b][:, P * q:P * q + P], g.ident[:, :])
                mm.then_inc(tx[b], 1)

            for b in range(2):
                pe.sem_inc(gu[b], 1)
                pe.sem_inc(th[b], 1)
                pe.sem_inc(dn[b], 1)
            for b in range(2):
                pe.wait_ge(x_ld[b], 16)
                if b:
                    pe.wait_ge(xga[0], 1)
                    pe.wait_ge(xgd[0], 1)
                turn_rows(b)
            with pe.Fori(0, NPAIR) as i:
                with pe.If(i < n):
                    for b in range(2):
                        pe.wait_ge(wg_ld[b], 16 * i + 16)
                        pe.wait_ge(xga[b], i + 1)
                        pe.wait_ge(xgd[b], i + 1)
                        pe.wait_ge(hd[b], i + 1)
                        for k in range(KC):
                            mm = pe.matmul(g.bank[1][:, b, :], xg[b][:, k, :], wg[b][:, k, :], start=(k == 0), stop=(k == KC - 1))
                        mm.then_inc(gu[b], 1)
                    for b in range(2):
                        pe.wait_ge(hd[b], i + 2)
                        pe.wait_ge(hte[1 - b], i + 1 + b)
                        for q in range(2):
                            mm = pe.transpose(g.pb6[:, P * q:P * q + P], hid[b][:, P * q:P * q + P], g.ident[:, :])
                        mm.then_inc(th[b], 1)
                        pe.wait_ge(x_ld[b], 16 * i + 32)
                        if b:
                            pe.wait_ge(xga[0], i + 2)
                            pe.wait_ge(xgd[0], i + 2)
                        turn_rows(b)
                        pe.wait_ge(hte[b], i + 2)
                        pe.wait_ge(wd_ld[b], 16 * i + 16)
                        pe.wait_ge(ya[1 - b], i + 1 + b)
                        pe.wait_ge(yd[1 - b], i + 1 + b)
                        for half in range(2):
                            for q in range(2):
                                mm = pe.matmul(g.pt[:, half, :], hT[b][:, P * q:P * q + P], wd[b][:, q, 512 * half:512 * half + 512],
                                               start=(q == 0), stop=(q == 1))
                        mm.then_inc(dn[b], 1)

        @block.scalar
        def _(act):
            n = count(act)
            rows = lambda b: act.activation(xg[b][:, 0:4, :].rearrange("p a b -> p (a b)"), g.bank[0][:, 0, :], ACT.Copy)
            for b in range(2):
                act.sem_inc(ya[b], 1)
                act.sem_inc(hte[b], 1)
                act.sem_inc(y_st[b], 16)
            for b in range(2):
                act.wait_ge(tx[b], 1)
                rows(b).then_inc(xga[b], 1)
            with act.Fori(0, NPAIR) as i:
                with act.If(i < n):
                    for b in range(2):
                        act.wait_ge(gu[b], i + 2)
                        act.wait_ge(hd[b], i + 1)
                        act.activation(sg[b][:, :], g.bank[1][:, b, 0:FF], ACT.Silu).then_inc(sil[b], 1)
                    for b in range(2):
                        act.wait_ge(th[b], i + 2)
                        act.activation(hT[b][:, :], g.pb6[:, 0:FF], ACT.Copy).then_inc(hte[b], 1)
                        act.wait_ge(tx[b], i + 2)
                        rows(b).then_inc(xga[b], 1)
                        act.wait_ge(dn[b], i + 2)
                        act.wait_ge(y_st[b], 16 * i + 16)
                        act.activation(y[b][:, 0:512], g.pt[:, 0, :], ACT.Copy).then_inc(ya[b], 1)
                        act.wait_ge(ya[b], i + 2)
                        act.wait_ge(yd[b], i + 2)
                        act.dma_start(g.xs_rows[bass.ds((2 * i + b) * P, P), :], y[b][:, :]).then_inc(y_st[b], 16)

        @block.gpsimd
        def _(pool):
            n = count(pool)
            for b in range(2):
                pool.wait_ge(y_st[b], 16 * n + 16)

        @block.vector
        def _(dve):
            n = count(dve)
            rows = lambda b: dve.tensor_copy(xg[b][:, 4:8, :].rearrange("p a b -> p (a b)"), g.bank[0][:, 1, :])
            for b in range(2):
                dve.sem_inc(hd[b], 1)
                dve.sem_inc(yd[b], 1)
            for b in range(2):
                dve.wait_ge(tx[b], 1)
                rows(b).then_inc(xgd[b], 1)
            with dve.Fori(0, NPAIR) as i:
                with dve.If(i < n):
                    for b in range(2):
                        dve.wait_ge(sil[b], i + 1)
                        dve.wait_ge(th[b], i + 1)
                        dve.tensor_tensor(hid[b][:, :], sg[b][:, :], g.bank[1][:, b, FF:2 * FF], ALU.mult).then_inc(hd[b], 1)
                    for b in range(2):
                        dve.wait_ge(tx[b], i + 2)
                        rows(b).then_inc(xgd[b], 1)
                        dve.wait_ge(dn[b], i + 2)
                        dve.wait_ge(y_st[b], 16 * i + 16)
                        dve.tensor_copy(y[b][:, 512:D], g.pt[:, 1, :]).then_inc(yd[b], 1)


def stage_combine(nc, g, t, l, m, last):
    with ExitStack() as ctx:
        sb = lambda name, shape, dt=F32: ctx.enter_context(nc.sbuf_tensor(f"c{l}_{name}", shape, dt))
        sem = lambda name: g.sem(f"c{l}_{name}")
        yk = sb("yk", [P, TT, 2, D])
        z = sb("z", [P, 2, D])
        sq, root_t, rstd = sb("sq", [P, 2, NT]), sb("root", [P, NT]), sb("rstd", [P, NT])
        n = norm_sems(g, f"c{l}")
        yl = [sem(f"yl{i}") for i in range(TT)]
        zr, tz, res, ch, ost = sem("zr"), sem("tz"), sem("res"), sem("ch"), sem("ost")
        block = ctx.enter_context(nc.Block())

        @block.sync
        def _(sp):
            if l == 0:
                sp.dma_start(g.wbig[:, :, 0:768], t["mla_win"]).then_inc(g.wbig_ld, 16)
            if last:
                for k in range(KC):
                    sp.wait_ge(n.aff, k + 1)
                    sp.dma_start(t["yT"][:, k, :], g.hT[:, k, :]).then_inc(ost, 16)
                sp.wait_ge(ost, 16 * KC)

        @block.gpsimd
        def _(pool):
            for i in range(TT):
                for k in range(2):
                    pool.indirect_dma_start(yk[:, i, k, :], None, g.xs_rows[:, :],
                                            bass.IndirectOffsetOnAxis(m.slot[:, k, i:i + 1], 0)).then_inc(yl[i], 16)
            if not last:
                apply_pool(pool, g, n, l + 1, 0)

        @block.vector
        def _(dve):
            def residual(i):
                dve.wait_ge(tz, i + 1)
                for k in range(KC):
                    c = 0 if i < TT - 1 else 1
                    ins = dve.scalar_tensor_tensor(out=g.xT[:, k, P * i:P * i + P],
                                                   in0=g.bank[i % 2][:, k // 4, P * (k % 4):P * (k % 4) + P],
                                                   scalar=g.modc[:, l, c, 40 + k:41 + k], in1=g.xT[:, k, P * i:P * i + P],
                                                   op0=ALU.mult, op1=ALU.add)
                ins.then_inc(res, 1)
            c = Chain(dve, ch)
            for i in range(TT):
                dve.wait_ge(yl[i], 32)
                if i >= 2:
                    dve.wait_ge(tz, i - 1)
                c.step(dve.tensor_scalar(z[:, i % 2, :], yk[:, i, 0, :], m.w12[:, 0, i, 0:1], None, ALU.mult))
                dve.scalar_tensor_tensor(out=z[:, i % 2, :], in0=yk[:, i, 1, :], scalar=m.w12[:, 1, i, 0:1],
                                         in1=z[:, i % 2, :], op0=ALU.mult, op1=ALU.add).then_inc(zr, 1)
                if i >= 1:
                    residual(i - 1)
            residual(TT - 1)
            apply_dve(dve, g, root_t, rstd, n, l + 1, None if last else 0)

        @block.tensor
        def _(pe):
            for i in range(TT):
                pe.wait_ge(zr, i + 1)
                if i >= 2:
                    pe.wait_ge(res, i - 1)
                for k in range(KC):
                    mm = pe.transpose(g.bank[i % 2][:, k // 4, P * (k % 4):P * (k % 4) + P], z[:, i % 2, P * k:P * k + P],
                                      g.ident[:, :])
                mm.then_inc(tz, 1)
            for k in range(KC):
                stat_matmul(pe, g, sq, k, KC - 1, n)

        @block.scalar
        def _(act):
            act.wait_ge(res, TT)
            for k in range(KC):
                square(act, g, sq, k, g.xT[:, k, :], n)
            root(act, g, root_t, n)
            if not last:
                apply_act(act, g, n, l + 1, 0)
            else:
                for k in range(KC):
                    act.wait_ge(n.mul, k + 1)
                    act.activation(g.hT[:, k, :], g.hT[:, k, :], ACT.Copy, scale=g.cols[:, 96 + 32 + k:97 + 32 + k])\
                        .then_inc(n.aff, 1)


def stage_mla_in(nc, g, t, a):
    with ExitStack() as ctx:
        sb = lambda name, shape, dt=F32: ctx.enter_context(nc.sbuf_tensor("i_" + name, shape, dt))
        sem = lambda name: g.sem("i_" + name)
        raw = sb("raw", [P, 5, NT])
        sq = sb("sq", [P, 2, NT])
        rt, rs = sb("rt", [P, 2, NT]), sb("rs", [P, 2, NT])
        t1, tab = sb("t1", [P, NT]), sb("tab", [P, NT])
        wuv = sb("wuv", [P, 2, D])
        front, ev, sqs, sts, rot, rcp, nrm, ld, vev, krs, vf, ost = (sem(k) for k in (
            "front", "ev", "sqs", "sts", "rot", "rcp", "nrm", "ld", "vev", "krs", "vf", "ost"))
        sld, ch, krt = sem("sld"), sem("ch"), sem("krt")
        free = [sem(f"free{s}") for s in range(2)]
        block = ctx.enter_context(nc.Block())
        gains = g.cols[:, 96 + 5 * KC:96 + 5 * KC + 5]
        last_of = {2: 0, 4: 1}

        @block.sync
        def _(sp):
            sp.dma_start(tab[:, :], t["mla_kr_tab"]).then_inc(ld, 16)
            sp.dma_start(wuv[:, :, :], t["mla_wuv"]).then_inc(ld, 16)
            sp.dma_start(a.ckvT[:, :, NT:KEYS], t["mla_ckvT"]).then_inc(ld, 16)
            for b in range(2):
                sp.dma_start(a.kx[b][1][0:64, NT:KEYS], t["mla_krT"][0:64]).then_inc(ld, 16)
                sp.dma_start(a.kx[b][0][64:P, NT:KEYS], t["mla_krT"][64:P]).then_inc(ld, 16)
            sp.dma_start(a.tab[:, :, :], t["mla_q_tab"]).then_inc(ld, 16)
            sp.dma_start(a.wuk[:, :, :], t["mla_wuk"]).then_inc(ld, 16)
            sp.wait_ge(nrm, 5)
            sp.dma_start(t["new_ckvT"], a.ckvT[:, :, NL:NT]).then_inc(ost, 16)
            sp.wait_ge(krs, 1)
            sp.dma_start(t["new_krT"], a.kx[0][0][64:96, NL:NT]).then_inc(ost, 16)
            sp.wait_ge(ost, 32)
            sp.wait_ge(front, 6)
            sp.dma_start(g.wbig[:, :, :], t["mla_wo"]).then_inc(g.wbig_ld, 16)

        @block.tensor
        def _(pe):
            def stat(c):
                pe.wait_ge(sqs, c + 1)
                z = 0 if c < 3 else 1
                s, e = c in (0, 3), c in (2, 4)
                big, small = (g.pt[:, 0, :], g.pt[:, 1, 0:NC_]) if z == 0 else (g.pb6[:, :], g.pb7[:, 0:NC_])
                pe.matmul(big, g.ones[:, :], sq[:, c % 2, 0:NL], start=s, stop=e)
                pe.matmul(small, g.ones[:, :], sq[:, c % 2, NL:NT], start=s, stop=e).then_inc(sts, 1)
            pe.wait_ge(g.wbig_ld, 48)
            for c in range(6):
                if c >= 2:
                    pe.wait_ge(free[c % 2], c // 2)
                for lo, hi, z in spans():
                    for k in range(KC):
                        mm = pe.matmul(g.bank[c % 2][:, z, 0:hi - lo], g.wbig[:, k, P * c:P * c + P], g.hT[:, k, lo:hi],
                                       start=(k == 0), stop=(k == KC - 1))
                mm.then_inc(front, 1)
                if c >= 1:
                    stat(c - 1)
            pe.wait_ge(nrm, 5)
            pe.wait_ge(ld, 16 * 9)
            for i in range(TT + 1):
                u = 6 + i
                pe.wait_ge(free[u % 2], u // 2)
                for half in range(2):
                    for k in range(2):
                        mm = pe.matmul(g.bank[u % 2][:, half, :], a.ckvT[:, k, P * i:P * i + P],
                                       wuv[:, k, 512 * half:512 * half + 512], start=(k == 0), stop=(k == 1))
                mm.then_inc(front, 1)

        @block.vector
        def _(dve):
            for c in range(5):
                dve.wait_ge(front, c + 1)
                dve.tensor_copy(raw[:, c, :], slot2(g, c % 2)[:, 0:NT]).then_inc(free[c % 2], 1)
                dve.wait_ge(free[c % 2], c // 2 + 1)
                dve.sem_inc(ev, 1)
            dve.wait_ge(front, 6)
            dve.wait_ge(ld, 16 * 9)
            src = slot2(g, 1)
            dve.tensor_tensor(t1[64:P, :], src[0:64, 0:NT], tab[0:64, :], ALU.mult).then_inc(krt, 1)
            dve.tensor_tensor(t1[0:64, :], src[64:P, 0:NT], tab[64:P, :], ALU.mult).then_inc(free[1], 1)
            dve.wait_ge(free[1], 3)
            dve.tensor_copy(a.kx[0][0][64:P, 0:NT], t1[0:64, :]).then_inc(krt, 1)
            dve.wait_ge(krt, 2)
            dve.tensor_tensor(a.kx[0][0][64:P, 0:NT], a.kx[0][0][64:P, 0:NT], t1[64:P, :], ALU.add).then_inc(krs, 1)
            for z in range(2):
                dve.wait_ge(rot, z + 1)
                dve.reciprocal(rs[:, z, :], rt[:, z, :]).then_inc(rcp, 1)
                dve.wait_ge(rcp, z + 1)
                for c in range(*((0, 3) if z == 0 else (3, 5))):
                    out = a.cqT[:, c, :] if z == 0 else a.ckvT[:, c - 3, 0:NT]
                    dve.scalar_tensor_tensor(out=out, in0=raw[:, c, :], scalar=gains[:, c:c + 1], in1=rs[:, z, :],
                                             op0=ALU.mult, op1=ALU.mult).then_inc(nrm, 1)
            for i in range(TT + 1):
                u = 6 + i
                dve.wait_ge(front, u + 1)
                dve.tensor_copy(a.V[:, i, :], slot2(g, u % 2)).then_inc(free[u % 2], 1)

        @block.scalar
        def _(act):
            for c in range(5):
                act.wait_ge(ev, c + 1)
                if c >= 2:
                    act.wait_ge(sts, c - 1)
                act.activation(sq[:, c % 2, :], raw[:, c, :], ACT.Square).then_inc(sqs, 1)
            act.wait_ge(sts, 3)
            act.activation(rt[:, 0, :], g.pt[:, :, :].rearrange("p a b -> p (a b)")[:, 0:NT], ACT.Sqrt,
                           bias=g.eps[:, 0:1], scale=1.0 / QR).then_inc(rot, 1)
            act.wait_ge(sts, 5)
            act.activation(rt[:, 1, 0:NL], g.pb6[:, :], ACT.Sqrt, bias=g.eps[:, 0:1], scale=1.0 / KVR)
            act.activation(rt[:, 1, NL:NT], g.pb7[:, 0:NC_], ACT.Sqrt, bias=g.eps[:, 0:1], scale=1.0 / KVR).then_inc(rot, 1)

        @block.gpsimd
        def _(pool):
            pool.wait_ge(krs, 1)
            pool.tensor_copy(a.kx[1][0][64:P, 0:NT], a.kx[0][0][64:P, 0:NT])
            for b in range(2):
                pool.tensor_copy(a.kx[b][1][0:64, 0:NT], a.kx[0][0][64:P, 0:NT])


def stage_mla(nc, g, t, a):
    with ExitStack() as ctx:
        sb = lambda name, shape, dt=F32: ctx.enter_context(nc.sbuf_tensor("m_" + name, shape, dt))
        sem = lambda name: g.sem("m_" + name)
        wuq = sb("wuq", [P, 2, 3, 2, P])
        q = [[sb(f"q{b}{h}", [P, NT]) for h in range(2)] for b in range(2)]
        S = sb("S", [P, 4, NT])
        PT = sb("PT", [P, 2, 2, NT])
        st = sb("st", [P, 4, 3])
        w_ld = [sem(f"w_ld{b}") for b in range(2)]
        free = [sem(f"free{s}") for s in range(2)]
        front, q_rdy, qw = sem("front"), sem("q_rdy"), sem("qw")
        k_rdy = sem("k_rdy")
        mn, ex, rcp, prob, tr, pta, ptd, pv = (sem(k) for k in ("mn", "ex", "rcp", "prob", "tr", "pta", "ptd", "pv"))
        oev = [sem(f"oev{s}") for s in range(2)]
        units = [("q", 0, 0), ("q", 0, 1), ("k", 0)]
        for p in range(PAIRS):
            nxt = [("q", p + 1, 0), ("q", p + 1, 1), ("k", p + 1)] if p + 1 < PAIRS else []
            units += [("s", p, n, h) for n in range(2) for h in range(2)] + nxt
            units += [("s", p, n, h) for n in range(2, 5) for h in range(2)]
        NA = 10 * PAIRS
        ntiles = lambda x: 5 if x % 10 < 8 else 1
        block = ctx.enter_context(nc.Block())

        @block.sync
        def _(sp):
            for p in range(PAIRS):
                if p >= 2:
                    sp.wait_ge(q_rdy, 2 * (p - 1))
                sp.dma_start(wuq[:, p % 2, :, :, :], t["mla_wuq"][p]).then_inc(w_ld[p % 2], 16)

        @block.tensor
        def _(pe):
            def slot_free(u):
                if u >= 2:
                    pe.wait_ge(free[u % 2], u // 2)

            def turn(x):
                pe.wait_ge(prob, x + 1)
                if x >= 1:
                    pe.wait_ge(pta, x)
                    pe.wait_ge(ptd, x)
                n = ntiles(x)
                for i in range(n):
                    mm = pe.transpose(g.pt[:, i // 3, P * (i % 3):P * (i % 3) + P], S[:, x % 4, P * i:P * i + P], g.ident[:, :])
                mm.then_inc(tr, 1)

            def weigh(b):
                p, n = b // 5, b % 5
                pe.wait_ge(pta, 2 * b + 2)
                pe.wait_ge(ptd, 2 * b + 2)
                if b >= 2:
                    pe.wait_ge(oev[b % 2], b // 2)
                tiles = [0, 1, 2, 3, TT] if n < 4 else [4]
                out = (g.pb6, g.pb7)[b % 2]
                for i, vt in enumerate(tiles):
                    for h in range(2):
                        mm = pe.matmul(out[64 * h:64 * h + 64, 0:P], a.V[:, vt, P * p + 64 * h:P * p + 64 * h + 64],
                                       PT[:, b % 2, h, P * i:P * i + P], start=(i == 0), stop=(i == len(tiles) - 1),
                                       tile_position=(0, 64 * h))
                mm.then_inc(pv, 1)

            x = 0
            for u, unit in enumerate(units):
                slot_free(u)
                bank = g.bank[u % 2]
                if unit[0] == "q":
                    p, h = unit[1:]
                    pe.wait_ge(w_ld[p % 2], 16 * (p // 2 + 1))
                    for lo, hi, c in spans():
                        for k in range(3):
                            mm = pe.matmul(bank[:, c, 0:hi - lo], wuq[:, p % 2, k, h, :], a.cqT[:, k, lo:hi],
                                           start=(k == 0), stop=(k == 2))
                    mm.then_inc(front, 1)
                elif unit[0] == "k":
                    p = unit[1]
                    for lo, hi, c in ((0, NL, 0), (NL, KEYS, 1)):
                        for k in range(2):
                            mm = pe.matmul(bank[:, c, 0:hi - lo], a.wuk[:, k, P * p:P * p + P], a.ckvT[:, k, lo:hi],
                                           start=(k == 0), stop=(k == 1))
                    mm.then_inc(front, 1)
                else:
                    p, n, h = unit[1:]
                    pe.wait_ge(q_rdy, 2 * (p + 1))
                    pe.wait_ge(k_rdy, 2 * (p + 1))
                    qb, kb = q[p % 2][h], a.kx[p % 2][h]
                    if n < 4:
                        pe.matmul(bank[:, 0, :], qb[:, P * n:P * n + P], kb[:, 0:NL], start=True, stop=True)
                        mm = pe.matmul(bank[:, 1, 0:P], qb[:, P * n:P * n + P], kb[:, NT:KEYS], start=True, stop=True)
                    else:
                        mm = pe.matmul(bank[:, 0, 0:P], qb[:, NL:NT], kb[:, NL:NT], start=True, stop=True)
                    mm.then_inc(front, 1)
                    if x >= 2:
                        turn(x - 2)
                    if x >= 4 and x % 2 == 0:
                        weigh((x - 4) // 2)
                    x += 1
            turn(NA - 2)
            weigh(NA // 2 - 2)
            turn(NA - 1)
            weigh(NA // 2 - 1)

        @block.vector
        def _(dve):
            def reciprocals(x):
                dve.wait_ge(ex, x + 1)
                dve.reciprocal(st[:, x % 4, 2:3], st[:, x % 4, 1:2]).then_inc(rcp, 1)
                dve.wait_ge(rcp, x + 1)
                w = P * ntiles(x)
                dve.tensor_scalar(S[:, x % 4, 0:w], S[:, x % 4, 0:w], st[:, x % 4, 2:3], None, ALU.mult).then_inc(prob, 1)

            def evacuate(x):
                dve.wait_ge(tr, x + 1)
                b, h = x // 2, x % 2
                if b >= 2:
                    dve.wait_ge(pv, b - 1)
                if ntiles(x) > 3:
                    dve.tensor_copy(PT[:, b % 2, h, 3 * P:5 * P], g.pt[:, 1, 0:2 * P]).then_inc(ptd, 1)
                else:
                    dve.sem_inc(ptd, 1)

            x = 0
            for u, unit in enumerate(units):
                if unit[0] == "q":
                    p, h = unit[1:]
                    dve.wait_ge(front, u + 1)
                    dve.tensor_tensor(q[p % 2][h][:, :], slot2(g, u % 2)[:, 0:NT], a.tab[:, h, :], ALU.mult)\
                        .then_inc(free[u % 2], 1)
                    dve.wait_ge(free[u % 2], u // 2 + 1)
                    dve.sem_inc(q_rdy, 1)
                elif unit[0] == "s":
                    w = P * ntiles(x)
                    dve.wait_ge(front, u + 1)
                    dve.tensor_reduce(st[:, x % 4, 0:1], slot2(g, u % 2)[:, 0:w], AX_X, ALU.min).then_inc(mn, 1)
                    if x >= 1:
                        reciprocals(x - 1)
                    if x >= 2:
                        evacuate(x - 2)
                    x += 1
            reciprocals(NA - 1)
            evacuate(NA - 2)
            evacuate(NA - 1)

        @block.scalar
        def _(act):
            def evacuate(x):
                act.wait_ge(tr, x + 1)
                b, h = x // 2, x % 2
                if b >= 2:
                    act.wait_ge(pv, b - 1)
                w = P * min(3, ntiles(x))
                act.activation(PT[:, b % 2, h, 0:w], g.pt[:, 0, 0:w], ACT.Copy).then_inc(pta, 1)

            def outputs(b):
                act.wait_ge(pv, b + 1)
                p, n = b // 5, b % 5
                act.activation(g.oT[:, p, P * n:P * n + P], (g.pb6, g.pb7)[b % 2][:, 0:P], ACT.Copy).then_inc(oev[b % 2], 1)

            x = 0
            for u, unit in enumerate(units):
                if unit[0] == "k":
                    p = unit[1]
                    act.wait_ge(front, u + 1)
                    act.activation(a.kx[p % 2][0][0:64, :], slot2(g, u % 2)[0:64, 0:KEYS], ACT.Copy).then_inc(k_rdy, 1)
                    act.activation(a.kx[p % 2][1][64:P, :], slot2(g, u % 2)[64:P, 0:KEYS], ACT.Copy).then_inc(free[u % 2], 1)
                    act.wait_ge(free[u % 2], u // 2 + 1)
                    act.sem_inc(k_rdy, 1)
                elif unit[0] == "s":
                    w = P * ntiles(x)
                    act.wait_ge(mn, x + 1)
                    if x >= 4:
                        act.wait_ge(tr, x - 3)
                    act.activation(S[:, x % 4, 0:w], slot2(g, u % 2)[:, 0:w], ACT.Exp, bias=st[:, x % 4, 0:1],
                                   scale=-1.0, accum_out=st[:, x % 4, 1:2]).then_inc(free[u % 2], 1)
                    act.wait_ge(free[u % 2], u // 2 + 1)
                    act.sem_inc(ex, 1)
                    if x >= 2:
                        evacuate(x - 2)
                    if x >= 5 and x % 2 == 1:
                        outputs((x - 5) // 2)
                    x += 1
            evacuate(NA - 2)
            outputs(NA // 2 - 2)
            evacuate(NA - 1)
            outputs(NA // 2 - 1)


def backbone(nc, t):
    with ExitStack() as ctx:
        g = declare(nc, ctx)
        with ExitStack() as early:
            g.ring = early.enter_context(nc.sbuf_tensor("ring", [P, 2, 2048], F32))
            with ExitStack() as first:
                stage_begin(nc, g, t)
                end_stage(nc, g)
            g.zero = early.enter_context(nc.sbuf_tensor("zero", [P, 256], F32))
            stage_na(nc, g, t)
            end_stage(nc, g)
        for l in range(2):
            if l == 1:
                with ExitStack() as mla:
                    a = Buffers()
                    sb = lambda name, shape: mla.enter_context(nc.sbuf_tensor("a_" + name, shape, F32))
                    a.V = sb("V", [P, TT + 1, D])
                    a.cqT, a.ckvT = sb("cqT", [P, 3, NT]), sb("ckvT", [P, 2, KEYS])
                    a.kx = [[sb(f"kx{b}{h}", [P, KEYS]) for h in range(2)] for b in range(2)]
                    a.tab = sb("tab", [P, 2, NT])
                    a.wuk = sb("wuk", [P, 2, D])
                    stage_mla_in(nc, g, t, a)
                    end_stage(nc, g)
                    stage_mla(nc, g, t, a)
                    end_stage(nc, g)
            stage_out(nc, g, t, l)
            end_stage(nc, g)
            with ExitStack() as moe:
                m = Buffers()
                m.w12 = moe.enter_context(nc.sbuf_tensor(f"w12_{l}", [P, 2, TT, 1], F32))
                m.slot = moe.enter_context(nc.sbuf_tensor(f"slot_{l}", [P, 2, TT], I32))
                m.jobs = moe.enter_context(nc.sbuf_tensor(f"jobs_{l}", [1, 34], I32))
                stage_route(nc, g, t, l, m)
                end_stage(nc, g)
                stage_experts(nc, g, t, l, m)
                end_stage(nc, g)
                stage_combine(nc, g, t, l, m, l == 1)
                end_stage(nc, g)


def token_order():
    n = np.arange(NL)
    tile, row, col = n // P, n % P // QB, n % QB
    return row * GRID_W + tile * QB + col


def constants():
    order = token_order()
    ident = np.eye(P, dtype=np.float32)
    inv = (1.0 / (np.float32(10000.0) ** (np.arange(8, dtype=np.float32) / np.float32(8)))).astype(np.float32)
    ang = np.concatenate([(order // GRID_W)[:, None].astype(np.float32) * inv,
                          (order % GRID_W)[:, None].astype(np.float32) * inv], axis=1)
    cos, sin = np.cos(ang).T.astype(np.float32), np.sin(ang).T.astype(np.float32)
    cosd, sind = np.ones((32, NT), np.float32), np.zeros((32, NT), np.float32)
    cosd[:, :NL] = np.concatenate([cos, cos])
    sind[:, :NL] = np.concatenate([-sin, sin])
    s = np.float32(-MLA_SCALE)
    nope = np.full((64, NT), s, np.float32)
    q_tab = np.stack([np.concatenate([nope, cosd * s, sind * s]), np.concatenate([cosd * s, sind * s, nope])], 1)
    kr_tab = np.concatenate([sind, sind, cosd, cosd])
    c = (np.arange(P) % QB)[:, None]
    kc = (np.arange(P) % QB)[None, :]
    off = lambda rel: kc + QB * rel - c
    out = lambda ok: np.where(ok, 0.0, BIG).astype(np.float32)
    mask = np.stack([out((off(r) >= -8) & (off(r) < 8)) for r in (-1, 0, 1)], 1)
    first = np.clip(c - 8, 0, None)
    last = np.clip(c - 8, None, 0)
    mask_e = np.stack([out((kc >= first) & (kc < first + QB)), out((kc >= last) & (kc < last + QB))], 1)
    cst = np.zeros((P, 3 * P), np.float32)
    cst[:, 0:32] = np.arange(32)
    cst[:, 32:37] = SLOT * np.arange(5)
    cst[:, 40:56] = 2 * np.arange(16)
    i = np.arange(P)
    cst[:, P:2 * P] = i[:, None] < i[None, :]
    e = np.arange(NE)
    cst[:NE, 2 * P:2 * P + NE] = SLOT * (e[:, None] < e[None, :])
    cst[:NE, 2 * P + NE:2 * P + 2 * NE] = e[:, None] <= e[None, :]
    return dict(ident=ident, mask=mask, mask_e=mask_e, cst=cst, mla_q_tab=q_tab, mla_kr_tab=kr_tab)


def layout(x):
    order = token_order()
    a = {}
    chunks = lambda w: w.reshape(-1, P, w.shape[-1]).transpose(1, 0, 2)
    tokens = np.concatenate([x["x_sample"][0][order], x["x_prompt"][0]])
    a["xT"] = chunks(tokens.T)
    a["c2"] = chunks(np.stack([x["c"][0], x["c_ctx"]], 1))
    a["ada_w"] = x["ada_w"].reshape(2, KC, P, 3, 2048).transpose(0, 3, 1, 2, 4)
    col = lambda v: v.reshape(-1, P).T
    a["cols"] = np.concatenate([col(x["ada_b"][0]), col(x["ada_b"][1]), col(x["norm_mix_g"][0]), col(x["norm_ffn_g"][0]),
                                col(x["norm_mix_g"][1]), col(x["norm_ffn_g"][1]), col(x["final_norm_g"]),
                                col(x["mla_q_norm_g"][0]), col(x["mla_kv_norm_g"][0])], 1)
    qkv = x["na_w_qkv"][0].reshape(KC, P, 3, PAIRS, P)
    a["na_wqk"] = qkv[:, :, 0:2].transpose(3, 2, 1, 0, 4).reshape(2 * PAIRS, P, KC, P)
    a["na_wv"] = chunks(x["na_w_qkv"][0][:, 2 * D:])
    a["na_wo"] = chunks(x["na_w_o"][0])
    a["na_kcT"] = chunks(x["state_na_k"][0, 0].reshape(P, D).T)
    a["na_vc"] = x["state_na_v"][0, 0].reshape(P, D)
    rpb = np.zeros((NA_H * 15, 64), np.float32)
    rpb[:, 16:47] = x["na_rpb"][0].reshape(NA_H * 15, 31)
    a["rpb"] = rpb
    w_in = x["mla_w_in"][0]
    kr = w_in[:, QR + KVR:]
    swap = np.concatenate([kr[:, 16:], kr[:, :16]], 1)
    a["mla_win"] = chunks(np.concatenate([w_in[:, :QR + KVR], swap, swap, kr, kr], 1))
    uq = x["mla_w_uq"][0].reshape(3, P, 16, 96)
    nope, rope = uq[..., :64], uq[..., 64:]
    rswap = np.concatenate([rope[..., 16:], rope[..., :16]], -1)
    even, odd = np.concatenate([nope, rope, rswap], -1), np.concatenate([rope, rswap, nope], -1)
    a["mla_wuq"] = np.stack([even[:, :, 0::2], odd[:, :, 1::2]], 3).transpose(2, 1, 0, 3, 4)
    a["mla_wuk"], a["mla_wuv"] = chunks(x["mla_w_uk"][0]), chunks(x["mla_w_uv"][0])
    a["mla_wo"] = chunks(x["mla_w_o"][0])
    a["mla_ckvT"] = chunks(x["state_mla_ckv"][0, 0].T)
    a["mla_krT"] = np.concatenate([x["state_mla_kr"][0, 0].T] * 4)
    a["rw"] = np.stack([chunks(np.concatenate([x["moe_w_group"][l], x["moe_w_expert"][l]], 1)) for l in range(2)], 1)
    a["rb"] = np.concatenate([x["moe_b_group"], x["moe_b_expert"]], 1)[None]
    gu = np.concatenate([x["moe_w_gate"], x["moe_w_up"]], -1)
    a["moe_gu"] = gu.reshape(2, NE, KC, P, 2 * FF).transpose(0, 1, 3, 2, 4).reshape(2, NE, P, KC * 2 * FF)
    a["moe_dn"] = x["moe_w_down"].reshape(2, NE, 2, P, D).transpose(0, 1, 3, 2, 4).reshape(2, NE, P, 2 * D)
    return a


_OUTS = {"yT": [P, KC, NT], "new_kT": [PAIRS, P, NC_], "new_v": [NC_, D], "new_ckvT": [P, 2, NC_], "new_krT": [ROPE, NC_]}


def kernel(**inputs):
    import concourse.bacc as _bacc
    from concourse.bass_utils import run_bass_kernel_spmd as _run

    x = {k: np.asarray(v) for k, v in inputs.items()}
    arrays = {f"in_{k}": np.ascontiguousarray(v) for k, v in {**layout(x), **constants()}.items()}
    nc = _bacc.Bacc("TRN2", target_bir_lowering=False, num_devices=1)
    t = {}
    for k, v in arrays.items():
        t[k[3:]] = nc.dram_tensor(k, v.shape, mybir.dt.from_np(v.dtype), kind="ExternalInput").ap()
    for k, shape in _OUTS.items():
        t[k] = nc.dram_tensor(f"out_{k}", shape, F32, kind="ExternalOutput").ap()
    backbone(nc, t)
    r = _run(nc, [arrays], core_ids=[0]).results[0]
    y = r["out_yT"].transpose(2, 1, 0).reshape(NT, D)
    sample = np.empty((NL, D), np.float32)
    sample[token_order()] = y[:NL]
    new_k = r["out_new_kT"].reshape(D, NC_).T.reshape(1, 1, NC_, NA_H, NA_DH)
    new_v = r["out_new_v"].reshape(1, 1, NC_, NA_H, NA_DH)
    ckv = r["out_new_ckvT"].transpose(2, 1, 0).reshape(1, 1, NC_, KVR)
    kr = r["out_new_krT"].T.reshape(1, 1, NC_, ROPE)
    return (y[NL:].reshape(1, NC_, D), sample.reshape(1, NL, D), np.ascontiguousarray(new_k), new_v,
            np.ascontiguousarray(ckv), np.ascontiguousarray(kr))
```
